# Optimizing a Trainium2 kernel written in Bass

```python
import math
import jax, jax.numpy as jnp
from jax import lax
import numpy as np

D_MODEL = 1024
BATCH = 1
SEQ = 512
DEPTH = 2

GRID_W = 64
CTX_LEN = 256
Q_BLOCK = 128
ROPE_THETA = 10000.0
EPS = 1e-6

GQA_HEADS = 6
GQA_KV_HEADS = 2
GQA_HEAD_DIM = 64
GQA_WIDTH = GQA_HEADS * GQA_HEAD_DIM
DIFF_HEADS = 4
DIFF_QK_DIM = 32
DIFF_V_DIM = 64
DIFF_WIDTH = DIFF_HEADS * DIFF_V_DIM
MLA_HEADS = 6
MLA_NOPE = 64
MLA_ROPE = 32
MLA_V = 64
MLA_Q_RANK = 192
MLA_KV_RANK = 128
MLA_WIDTH = MLA_HEADS * MLA_V
MIX_WIDTH = GQA_WIDTH + DIFF_WIDTH + MLA_WIDTH

IN_SIZES = (
    GQA_HEADS * GQA_HEAD_DIM,
    GQA_KV_HEADS * GQA_HEAD_DIM,
    GQA_KV_HEADS * GQA_HEAD_DIM,
    2 * DIFF_HEADS * DIFF_QK_DIM,
    2 * DIFF_HEADS * DIFF_QK_DIM,
    DIFF_HEADS * DIFF_V_DIM,
    MLA_Q_RANK,
    MLA_KV_RANK,
    MLA_ROPE,
    GQA_WIDTH,
    DIFF_WIDTH,
    MLA_WIDTH,
)
IN_COLS = int(sum(IN_SIZES))
IN_SPLITS = tuple(int(s) for s in np.cumsum(IN_SIZES)[:-1])

DEEPNORM_ALPHA = (2.0 * DEPTH) ** 0.25
DEEPNORM_BETA = (8.0 * DEPTH) ** -0.25
GQA_SCALE = GQA_HEAD_DIM ** -0.5
DIFF_SCALE = DIFF_QK_DIM ** -0.5
MLA_SCALE = (MLA_NOPE + MLA_ROPE) ** -0.5

kernel_name = "hybrid_parallel_heads_dit_block"

def rms_norm(x, g):
    xf = x.astype(jnp.float32)
    y = xf * lax.rsqrt(jnp.mean(xf * xf, axis=-1, keepdims=True) + EPS)
    return (y * g.astype(jnp.float32)).astype(x.dtype)

def layer_norm(x, g=None, b=None):
    xf = x.astype(jnp.float32)
    mu = jnp.mean(xf, axis=-1, keepdims=True)
    var = jnp.mean(jnp.square(xf - mu), axis=-1, keepdims=True)
    y = (xf - mu) * lax.rsqrt(var + EPS)
    if g is not None:
        y = y * g.astype(jnp.float32) + b.astype(jnp.float32)
    return y.astype(x.dtype)

def rope_tables(pos, dim, dtype):
    freqs = ROPE_THETA ** (-jnp.arange(0, dim, 2, dtype=jnp.float32) / dim)
    ang = pos.astype(jnp.float32)[:, None] * freqs[None, :]
    return (jnp.cos(ang).astype(dtype), jnp.sin(ang).astype(dtype))

def axial_tables(row, col, head_rot_dim, dtype):
    half = head_rot_dim // 2
    return rope_tables(row, half, dtype) + rope_tables(col, half, dtype)

def rope_rotate(x, cos, sin):
    a, b = jnp.split(x, 2, axis=-1)
    cs = cos[None, :, None, :]
    sn = sin[None, :, None, :]
    return jnp.concatenate([a * cs - b * sn, a * sn + b * cs], axis=-1)

def axial_rope(x, tabs):
    cos_r, sin_r, cos_c, sin_c = tabs
    xr, xc = jnp.split(x, 2, axis=-1)
    return jnp.concatenate([rope_rotate(xr, cos_r, sin_r), rope_rotate(xc, cos_c, sin_c)], axis=-1)

def block_attention(q, k, v, scale):
    B, S, H, dq = q.shape
    Hk = k.shape[2]
    G = H // Hk
    nb = S // Q_BLOCK
    qb = jnp.moveaxis(q.reshape(B, nb, Q_BLOCK, Hk, G, dq), 1, 0)

    def one_block(qblk):
        s = jnp.einsum('bqkgd,blkd->bkgql', qblk, k).astype(jnp.float32) * scale
        p = jax.nn.softmax(s, axis=-1).astype(v.dtype)
        return jnp.einsum('bkgql,blkd->bqkgd', p, v)

    o = lax.map(one_block, qb)
    return jnp.moveaxis(o, 0, 1).reshape(B, S, H, v.shape[-1])

def gqa_q(z, g, tabs):
    B, L, _ = z.shape
    q = rms_norm(z.reshape(B, L, GQA_HEADS, GQA_HEAD_DIM), g)
    return q if tabs is None else axial_rope(q, tabs)

def gqa_kv(zk, zv, g, tabs):
    B, L, _ = zk.shape
    k = rms_norm(zk.reshape(B, L, GQA_KV_HEADS, GQA_HEAD_DIM), g)
    if tabs is not None:
        k = axial_rope(k, tabs)
    return k, zv.reshape(B, L, GQA_KV_HEADS, GQA_HEAD_DIM)

def diff_qk(z, tabs):
    B, L, _ = z.shape
    t = z.reshape(B, L, 2 * DIFF_HEADS, DIFF_QK_DIM)
    if tabs is not None:
        t = axial_rope(t, tabs)
    return t[:, :, 0::2], t[:, :, 1::2]

def diff_v(z):
    B, L, _ = z.shape
    return z.reshape(B, L, DIFF_HEADS, DIFF_V_DIM)

def diff_out(o1, o2, lam, lam_init, subln_g):
    o = o1 - lam.astype(o1.dtype) * o2
    return rms_norm(o, subln_g) * (1.0 - lam_init)

def mla_q(zcq, g, w_uq, tabs):
    B, L, _ = zcq.shape
    q = (rms_norm(zcq, g) @ w_uq).reshape(B, L, MLA_HEADS, MLA_NOPE + MLA_ROPE)
    q_nope, q_pe = jnp.split(q, [MLA_NOPE], axis=-1)
    if tabs is not None:
        q_pe = axial_rope(q_pe, tabs)
    return jnp.concatenate([q_nope, q_pe], axis=-1)

def mla_kv(zckv, zkr, g, w_ukv, tabs):
    B, L, _ = zckv.shape
    kv = (rms_norm(zckv, g) @ w_ukv).reshape(B, L, MLA_HEADS, MLA_NOPE + MLA_V)
    k_nope, v = jnp.split(kv, [MLA_NOPE], axis=-1)
    k_pe = zkr.reshape(B, L, 1, MLA_ROPE)
    if tabs is not None:
        k_pe = axial_rope(k_pe, tabs)
    k = jnp.concatenate([k_nope, jnp.broadcast_to(k_pe, (B, L, MLA_HEADS, MLA_ROPE))], axis=-1)
    return k, v

def merge_groups(o_a, o_b, o_c, g_a, g_b, g_c, w_out):
    B, L = o_a.shape[:2]
    h = jnp.concatenate([
        o_a.reshape(B, L, GQA_WIDTH) * jax.nn.silu(g_a),
        o_b.reshape(B, L, DIFF_WIDTH) * jax.nn.silu(g_b),
        o_c.reshape(B, L, MLA_WIDTH) * jax.nn.silu(g_c),
    ], axis=-1)
    return h @ w_out

def hybrid_layer(xl, xc, c, c_ctx, p, lam_init, tabs64, tabs32, ctx_out):
    sh_l, sc_l, gt_l = jnp.split(jax.nn.silu(c) @ p["w_ada"] + p["b_ada"], 3, axis=-1)
    sh_c, sc_c, gt_c = jnp.split(jax.nn.silu(c_ctx) @ p["w_ada"] + p["b_ada"], 3, axis=-1)
    hl = layer_norm(xl) * (1 + sc_l[:, None, :]) + sh_l[:, None, :]
    hc = layer_norm(xc) * (1 + sc_c) + sh_c

    (gq_l, gk_l, gv_l, dq_l, dk_l, dv_l, mq_l, mkv_l, mkr_l, ga_l, gb_l, gc_l) = jnp.split(hl @ p["w_in"], IN_SPLITS, axis=-1)
    (gq_c, gk_c, gv_c, dq_c, dk_c, dv_c, mq_c, mkv_c, mkr_c, ga_c, gb_c, gc_c) = jnp.split(hc @ p["w_in"], IN_SPLITS, axis=-1)

    lam = (jnp.exp(jnp.sum(p["diff_lq1"].astype(jnp.float32) * p["diff_lk1"].astype(jnp.float32)))
           - jnp.exp(jnp.sum(p["diff_lq2"].astype(jnp.float32) * p["diff_lk2"].astype(jnp.float32)))
           + lam_init)

    kc_a, vc_a = gqa_kv(gk_c, gv_c, p["gqa_k_g"], None)
    k1c, k2c = diff_qk(dk_c, None)
    vc_b = diff_v(dv_c)
    kc_m, vc_m = mla_kv(mkv_c, mkr_c, p["mla_kv_g"], p["w_ukv"], None)

    ql_a = gqa_q(gq_l, p["gqa_q_g"], tabs64)
    kl_a, vl_a = gqa_kv(gk_l, gv_l, p["gqa_k_g"], tabs64)
    o_a = block_attention(ql_a, jnp.concatenate([kc_a, kl_a], 1), jnp.concatenate([vc_a, vl_a], 1), GQA_SCALE)

    q1l, q2l = diff_qk(dq_l, tabs32)
    k1l, k2l = diff_qk(dk_l, tabs32)
    v_all_b = jnp.concatenate([vc_b, diff_v(dv_l)], 1)
    o_b = diff_out(block_attention(q1l, jnp.concatenate([k1c, k1l], 1), v_all_b, DIFF_SCALE),
                   block_attention(q2l, jnp.concatenate([k2c, k2l], 1), v_all_b, DIFF_SCALE),
                   lam, lam_init, p["diff_subln_g"])

    ql_m = mla_q(mq_l, p["mla_q_g"], p["w_uq"], tabs32)
    kl_m, vl_m = mla_kv(mkv_l, mkr_l, p["mla_kv_g"], p["w_ukv"], tabs32)
    o_m = block_attention(ql_m, jnp.concatenate([kc_m, kl_m], 1), jnp.concatenate([vc_m, vl_m], 1), MLA_SCALE)

    y_l = merge_groups(o_a, o_b, o_m, ga_l, gb_l, gc_l, p["w_out"])
    xl_new = layer_norm(DEEPNORM_ALPHA * xl + gt_l[:, None, :] * y_l, p["ln_g"], p["ln_b"])
    if not ctx_out:
        return xl_new, None

    oc_a = block_attention(gqa_q(gq_c, p["gqa_q_g"], None), kc_a, vc_a, GQA_SCALE)
    q1c, q2c = diff_qk(dq_c, None)
    oc_b = diff_out(block_attention(q1c, k1c, vc_b, DIFF_SCALE),
                    block_attention(q2c, k2c, vc_b, DIFF_SCALE),
                    lam, lam_init, p["diff_subln_g"])
    oc_m = block_attention(mla_q(mq_c, p["mla_q_g"], p["w_uq"], None), kc_m, vc_m, MLA_SCALE)
    y_c = merge_groups(oc_a, oc_b, oc_m, ga_c, gb_c, gc_c, p["w_out"])
    xc_new = layer_norm(DEEPNORM_ALPHA * xc + gt_c * y_c, p["ln_g"], p["ln_b"])
    return xl_new, xc_new

def setup_inputs(seed: int = 0) -> dict:
    key = jax.random.key(seed)
    ks = jax.random.split(key, 21)

    def nrm(k, shape, s):
        return jax.random.normal(k, shape, jnp.float32) * s

    def gain(k, shape):
        return 1.0 + 0.02 * jax.random.normal(k, shape, jnp.float32)

    return {
        "x": nrm(ks[0], (BATCH, SEQ, D_MODEL), 1.0),
        "c": nrm(ks[1], (BATCH, D_MODEL), 1.0),
        "ctx": nrm(ks[2], (BATCH, CTX_LEN, D_MODEL), 1.0),
        "c_ctx": nrm(ks[3], (D_MODEL,), 1.0),
        "w_ada": nrm(ks[4], (DEPTH, D_MODEL, 3 * D_MODEL), 0.5 * D_MODEL ** -0.5),
        "b_ada": nrm(ks[5], (DEPTH, 3 * D_MODEL), 0.02),
        "w_in": nrm(ks[6], (DEPTH, D_MODEL, IN_COLS), D_MODEL ** -0.5),
        "gqa_q_g": gain(ks[7], (DEPTH, GQA_HEAD_DIM)),
        "gqa_k_g": gain(ks[8], (DEPTH, GQA_HEAD_DIM)),
        "diff_lq1": nrm(ks[9], (DEPTH, DIFF_QK_DIM), 0.1),
        "diff_lk1": nrm(ks[10], (DEPTH, DIFF_QK_DIM), 0.1),
        "diff_lq2": nrm(ks[11], (DEPTH, DIFF_QK_DIM), 0.1),
        "diff_lk2": nrm(ks[12], (DEPTH, DIFF_QK_DIM), 0.1),
        "diff_subln_g": gain(ks[13], (DEPTH, DIFF_V_DIM)),
        "mla_q_g": gain(ks[14], (DEPTH, MLA_Q_RANK)),
        "w_uq": nrm(ks[15], (DEPTH, MLA_Q_RANK, MLA_HEADS * (MLA_NOPE + MLA_ROPE)), MLA_Q_RANK ** -0.5),
        "mla_kv_g": gain(ks[16], (DEPTH, MLA_KV_RANK)),
        "w_ukv": nrm(ks[17], (DEPTH, MLA_KV_RANK, MLA_HEADS * (MLA_NOPE + MLA_V)), MLA_KV_RANK ** -0.5),
        "w_out": nrm(ks[18], (DEPTH, MIX_WIDTH, D_MODEL), DEEPNORM_BETA * MIX_WIDTH ** -0.5),
        "ln_g": gain(ks[19], (DEPTH, D_MODEL)),
        "ln_b": nrm(ks[20], (DEPTH, D_MODEL), 0.02),
    }

def reference(x, c, ctx, c_ctx, w_ada, b_ada, w_in, gqa_q_g, gqa_k_g, diff_lq1, diff_lk1, diff_lq2, diff_lk2,
              diff_subln_g, mla_q_g, w_uq, mla_kv_g, w_ukv, w_out, ln_g, ln_b):
    S = x.shape[1]
    ROWS = S // GRID_W
    row = jnp.repeat(jnp.arange(ROWS, dtype=jnp.int32), GRID_W)
    col = jnp.tile(jnp.arange(GRID_W, dtype=jnp.int32), ROWS)
    tabs64 = axial_tables(row, col, GQA_HEAD_DIM, x.dtype)
    tabs32 = axial_tables(row, col, DIFF_QK_DIM, x.dtype)

    xl, xc = x, ctx
    for i in range(DEPTH):
        p = {
            "w_ada": w_ada[i], "b_ada": b_ada[i], "w_in": w_in[i],
            "gqa_q_g": gqa_q_g[i], "gqa_k_g": gqa_k_g[i],
            "diff_lq1": diff_lq1[i], "diff_lk1": diff_lk1[i], "diff_lq2": diff_lq2[i], "diff_lk2": diff_lk2[i],
            "diff_subln_g": diff_subln_g[i],
            "mla_q_g": mla_q_g[i], "w_uq": w_uq[i], "mla_kv_g": mla_kv_g[i], "w_ukv": w_ukv[i],
            "w_out": w_out[i], "ln_g": ln_g[i], "ln_b": ln_b[i],
        }
        lam_init = 0.8 - 0.6 * math.exp(-0.3 * i)
        xl, xc = hybrid_layer(xl, xc, c, c_ctx, p, lam_init, tabs64, tabs32, i < DEPTH - 1)
    return xl


_drawn_inputs = setup_inputs


def setup_inputs(seed=0):
    import zlib

    import numpy as np

    out = dict(_drawn_inputs(seed))
    spreads = {}
    factors = {'ctx': 6.198,
     'c_ctx': 3.474,
     'b_ada': 8.0,
     'gqa_q_g': 8.0,
     'gqa_k_g': 8.0,
     'diff_lq1': 8.0,
     'diff_lk1': 8.0,
     'diff_lq2': 8.0,
     'diff_lk2': 8.0,
     'diff_subln_g': 8.0,
     'mla_q_g': 8.0,
     'w_uq': 8.0,
     'mla_kv_g': 8.0,
     'w_ukv': 4.22}
    for name, (base, spread) in spreads.items():
        noise = np.random.default_rng([zlib.crc32(name.encode()), seed]).standard_normal(out[name].shape)
        drawn = base * np.exp(spread * noise) if base else spread * noise
        out[name] = __import__('jax').numpy.asarray(drawn.astype(out[name].dtype))
    for name, factor in factors.items():
        out[name] = (out[name] * factor).astype(out[name].dtype)
    return out
```

```python
import math
from contextlib import ExitStack

import numpy as np

import concourse.bass as bass
from concourse import mybir

F32 = mybir.dt.float32
F32R = mybir.dt.float32r
ACT = mybir.ActivationFunctionType
ALU = mybir.AluOpType
AX = mybir.AxisListType

P = 128
D = 1024
KD = D // P
DEPTH = 2
NCTX, NLAT = 256, 512
NTOK = NCTX + NLAT
TILES = NTOK // P
CT = NCTX // P
GRID_W = 64
EPS = 1e-6
ALPHA = (2.0 * DEPTH) ** 0.25

GROUPS = [list(range(CT)), list(range(CT, TILES))]

CHUNKS = [
    [(0, 512)],
    [(512, 128), (1152, 256)],
    [(640, 512)],
    [(1408, 352)],
    [(1760, 512)],
    [(2272, 512)],
]
WIDTH = [sum(w for _, w in c) for c in CHUNKS]
CHUNK_ORDER = [0, 1, 2, 4, 3, 5]
RANK_Q, RANK_KV = 192, 128
UQ = 96
NUNIT = 20
NSLOT = 4
VH = 12
SCALE = {"gqa": 64 ** -0.5, "diff": 32 ** -0.5, "mla": 96 ** -0.5}


def family(u):
    return "gqa" if u < 6 else "diff" if u < 14 else "mla"


def value_head(u):
    return u // 3 if u < 6 else 2 + (u - 6) // 2 if u < 14 else u - 8


def gate_column(u):
    return 64 * u if u < 6 else 384 + 64 * ((u - 6) // 2) if u < 14 else 640 + 64 * (u - 14)


def blocks_of(u):
    return {0: (0, 3), 2: (1, None), 4: (2, None), 6: (4, 6), 10: (5, 7)}.get(u)


def q_tiles(L):
    return list(range(TILES)) if L < DEPTH - 1 else GROUPS[1]


def chunk_tiles(L, c):
    return GROUPS[1] if L == DEPTH - 1 and c >= 4 else list(range(TILES))


def chunk_cols(L, c, t):
    if L == DEPTH - 1 and t < CT:
        return {0: (256, 512), 1: (0, 384), 2: (256, 512), 3: (96, 352)}[c]
    return 0, WIDTH[c]


def score_steps(L):
    return list(range(TILES)) + (["ctx"] if L < DEPTH - 1 else [])


def count(keys):
    return {k: n + 1 for n, k in enumerate(keys)}


def transposed_blocks(L, first):
    return [("tp", L, b, g) for b in range(first, first + 4) for g in range(2)
            if not (L == DEPTH - 1 and g == 0 and b in (0, 1, 2, 4, 5))]


def compressed_blocks(L):
    return [("tc", L, j, g) for j in range(4) for g in range(2)
            if not (L == DEPTH - 1 and g == 0 and j < 2)]


def layer_uses(L):
    before = []
    if L == 0:
        before.append(("cT", L))
    before += [("ada", L, ch) for ch in range(6)] + [("adaT", L)]
    before += [("xT", L, g, k) for g in range(2) for k in range(KD)]
    for c in CHUNK_ORDER:
        before += [("z", L, c, t) for t in chunk_tiles(L, c)]
        if c == 1:
            before += transposed_blocks(L, 0)
        if c == 4:
            before += transposed_blocks(L, 4)
    before += compressed_blocks(L) + [("vm", L, t) for t in range(TILES)]
    gs = range(2) if L < DEPTH - 1 else [1]
    after = [("hT", L, g, k) for g in gs for k in range(KD)]
    after += [("gt", L, g, h) for g in gs for h in range(2)]
    after += [("y", L, h, t) for h in range(2) for t in q_tiles(L)]
    return before, after


USES, AFTER_ATTENTION = [], []
for _L in range(DEPTH):
    _b, _a = layer_uses(_L)
    USES += _b
    AFTER_ATTENTION.append(len(USES))
    USES += _a
USE = {k: n for n, k in enumerate(USES)}
BY_DVE = ("tp", "tc", "hT", "y", "adaT")
N_FREE_DVE = count([k for k in USES if k[0] in BY_DVE])
N_FREE_ACT = count([k for k in USES if k[0] not in BY_DVE])

PIECES, SLICES = [], []
for _L in range(DEPTH):
    PIECES += [("ada", _L, ch, kp) for ch in range(6) for kp in range(KD // 2)]
    for _c in CHUNK_ORDER:
        PIECES += [("in", _L, _c, kp) for kp in range(KD // 2)]
        SLICES += [("in", _L, _c, k) for k in range(KD)]
    PIECES += [("ukv", _L, 0, 0)] + [("uq", _L, j, 0) for j in range(2)]
    SLICES += [("ukv", _L, 0, 0)] + [("uq", _L, j, 0) for j in range(2)]
    PIECES += [("out", _L, h, kp) for h in range(2) for kp in range(KD // 2)]
    SLICES += [("out", _L, h, k) for h in range(2) for k in range(KD)]
PIECE = {k: n for n, k in enumerate(PIECES)}
NRAW = 3
N_SLICE = count(SLICES)
RING_SLICES = [s for s in SLICES if s[0] == "in" or (s[0] == "out" and s[2] == 0)]
RING_AT = {s: n for n, s in enumerate(RING_SLICES)}
N_USED = count([s for s in RING_SLICES if s[3] < KD - 1])
NW = 3


def piece_of(s):
    return (s[0], s[1], s[2], s[3] // 2)


def last_slice(p):
    return (p[0], p[1], p[2], 2 * p[3] + 1) if p[0] in ("in", "out") else p


N_ADA = count([p for p in PIECES if p[0] == "ada" and p[3] < KD // 2 - 1])
RAW_VALUE, _landed = {}, [0] * NRAW
for _n, _p in enumerate(PIECES):
    _landed[_n % NRAW] += 16 * (len(CHUNKS[_p[2]]) if _p[0] == "in" else 1)
    RAW_VALUE[_p] = _landed[_n % NRAW]

ROOTS = []
for _L in range(DEPTH):
    ROOTS += [("ln", _L, t) for t in range(TILES)]
    ROOTS += [("gqa", _L, t) for t in range(TILES)]
    ROOTS += [("mla", _L, t) for t in range(TILES)]
    ROOTS += [("diff", _L, u) for u in range(7, 14, 2)]
    ROOTS += [("out", _L, t) for t in q_tiles(_L)]
N_ROOT = count(ROOTS)

UNITS = [(L, u) for L in range(DEPTH) for u in range(NUNIT)]
UN = {k: n for n, k in enumerate(UNITS)}
N_UNIT = count(UNITS)


def mla_parts(L):
    return [("q", 1), ("k", 1)] + ([("q", 0)] if L < DEPTH - 1 else []) + [("k", 0)]


RING, MAXES, MROWS, OTRS, SPLITS, MLAS = [], [], [], [], [], []
STEPS = range(-4, NUNIT + 1)
for _L in range(DEPTH):
    for _i in STEPS:
        if 14 <= _i + 4 < NUNIT:
            MLAS.append((_L, _i + 4))
            RING += [(_L, _i + 4, "mla", p) for p in mla_parts(_L)]
        if 0 <= _i < NUNIT:
            RING += [(_L, _i, "s", s) for s in score_steps(_L)]
        if 0 <= _i + 2 < NUNIT:
            MAXES += [(_L, _i + 2, t) for t in q_tiles(_L)]
        if 0 <= _i + 4 < NUNIT and blocks_of(_i + 4):
            SPLITS.append((_L, _i + 4))
N_RINGB = count(RING)
N_MAX = count(MAXES)
N_SPLIT = count(SPLITS)
N_MLA = count(MLAS)
N_P = count([r for r in RING if r[2] == "s"])
N_RING_FREE = count([r for r in RING if r[2] == "mla"])
LATENTS_END = [N_P[L, u, "s", TILES - 1] for L, u in UNITS]
N_CTX = count([(L, u) for L, u in UNITS if L < DEPTH - 1])
UNIT_END = [N_P[L, u, "s", score_steps(L)[-1]] for L, u in UNITS]
N_GATE = count([(L, u) for L, u in UNITS if family(u) != "diff" or u % 2])
N_NORMED = count([(L, u) for L, u in UNITS if family(u) == "diff" and u % 2])
DMAS = {"gqa": 7, "diff": 7, "mla": 3}
STACKED = {}
for _n, (_L, _u) in enumerate(UNITS):
    STACKED[_n] = STACKED.get(_n - NSLOT, 0) + 16 * DMAS[family(_u)]


def hybrid_layers(nc, x, c, ctx_in, c_ctx, w_ada, b_ada, w_in, gqa_q_g, gqa_k_g, lam_vec, subln_g,
                  mla_q_g, w_uq, mla_kv_g, w_ukv, w_out, ln_g, ln_b, rope64, rope32, rope_t, out):
    x_mid = nc.dram_tensor("x_mid", (NTOK, D), F32).ap()

    with ExitStack() as stack:
        def sb(name, shape, dt=F32):
            return stack.enter_context(nc.sbuf_tensor(name, shape, dt))

        def sem(name):
            return stack.enter_context(nc.semaphore(name))

        area_a = sb("area_a", [P, 2 * KD * NTOK], F32R)
        area_b = sb("area_b", [P, KD * NTOK])
        area_g = sb("area_g", [P, TILES, D])
        cmp_t = sb("cmp_t", [P, 8, NTOK], F32R)
        vals = sb("vals", [P, TILES, VH, 65])
        w_split = sb("w_split", [P, NW, 2, 512], F32R)
        w_raw = sb("w_raw", [P, NRAW, 2, 512])
        ukv = sb("ukv", [P, 2, 768], F32R)
        area_z = sb("area_z", [P, TILES, 512])
        parts = sb("parts", [P, 4, NTOK], F32R)
        o_t = sb("o_t", [P, D])
        o_v = sb("o_v", [P, 2, TILES, 64])
        scr = sb("scr", [P, 2, 512])
        gate_row = sb("gate_row", [2, D])
        r64 = sb("r64", [P, 2, TILES - CT, 64])
        r32 = sb("r32", [P, 2, TILES - CT, 32])
        rt = sb("rt", [P, NLAT])
        gains = sb("gains", [P, DEPTH, 2, 64])
        mgain = sb("mgain", [P, DEPTH, RANK_Q + RANK_KV])
        sgain = sb("sgain", [P, DEPTH, 64])
        lam_in = sb("lam_in", [P, DEPTH, 4, 32])
        lam = sb("lam", [P, DEPTH, 4])
        ident = sb("ident", [P, P])
        sel = sb("sel", [2, 2, P])
        ones = sb("ones", [1, 2])
        ones_r = sb("ones_r", [1, P], F32R)
        c_silu = sb("c_silu", [P, 16])
        ada_col = sb("ada_col", [P, 16, 2])
        stats = sb("stats", [P, TILES, 2, 6])
        mean_var = sb("mean_var", [P, TILES, 2])
        var = sb("var", [P, 48])
        rstd = sb("rstd", [P, 48])
        half = sb("half", [P, 48])
        negmax = sb("negmax", [P, 2, TILES])
        m_row = sb("m_row", [TILES, 2, P], F32R)
        rec = sb("rec", [P, TILES])

        banks = stack.enter_context(nc.psum_tensor("banks", [P, 8, 512], F32))

        h_t = area_a[:].rearrange("p (s k n) -> p s k n", s=2, k=KD)
        slots = area_a[:].rearrange("p (s f n) -> p s f n", s=NSLOT, f=4)
        xb = area_b[:].rearrange("p (t d) -> p t d", t=TILES)
        qk_t = area_b[:].rearrange("p (b n) -> p b n", b=8)
        gates = area_g
        ends = area_g[:].rearrange("p t d -> p (t d)").rearrange("p (t d) -> p t d", d=D)
        ada_row = area_z[0:2].rearrange("p t n -> p (t n)")
        uq = w_split[0:UQ].rearrange("p a b n -> p (a b n)").rearrange("p (s j n) -> p s j n", s=2, j=2)
        b_row = o_t[0:1].rearrange("p (b n) -> p b n", b=2)
        c_rows = scr[0:16, 1, 0:P]
        ROW = {"gqa": 64, "diff": 96, "mla": 96}

        def bank(use):
            return banks[:, USE[use] % 8, :]

        consts_in = sem("consts_in")
        c_in = sem("c_in")
        x_in = sem("x_in")
        ends_in = sem("ends_in")
        bias_in = sem("bias_in")
        raw_in = [sem(f"raw_in{i}") for i in range(NRAW)]
        stack_in = [sem(f"stack_in{i}") for i in range(NSLOT)]
        mrow_in = [sem(f"mrow_in{i}") for i in range(NSLOT)]
        stored = sem("stored")
        pool_const = sem("pool_const")
        dve_const = sem("dve_const")
        w_hi = sem("w_hi")
        w_lo = sem("w_lo")
        w_used = sem("w_used")
        ada_used = sem("ada_used")
        filled = sem("filled")
        free_act = sem("free_act")
        free_dve = sem("free_dve")
        var_ready = sem("var_ready")
        root_ready = sem("root_ready")
        xn_ready = sem("xn_ready")
        h_ready = sem("h_ready")
        z_ready = sem("z_ready")
        hi_ready = sem("hi_ready")
        split_hi = sem("split_hi")
        split_lo = sem("split_lo")
        ring_filled = sem("ring_filled")
        ring_free = sem("ring_free")
        mla_roped = sem("mla_roped")
        mla_hi = sem("mla_hi")
        mla_lo = sem("mla_lo")
        max_filled = sem("max_filled")
        max_read = sem("max_read")
        mt_filled = sem("mt_filled")
        mrow_ready = sem("mrow_ready")
        p_ready = sem("p_ready")
        p_used = sem("p_used")
        o_copied = sem("o_copied")
        ctx_copied = sem("ctx_copied")
        ot_filled = sem("ot_filled")
        o_read = sem("o_read")
        normed = sem("normed")
        gated = sem("gated")
        lam_dots = sem("lam_dots")
        lam_exp = sem("lam_exp")
        x_new = sem("x_new")
        scaled = sem("scaled")
        dve_seq = sem("dve_seq")
        act_seq = sem("act_seq")
        pool_seq = sem("pool_seq")

        NH = [k for k in USES if k[0] == "xT"]
        N_H = count([k[1:] for k in NH])
        N_Z = count([(L, c_, t) for L in range(DEPTH) for c_ in (0, 2, 3) for t in range(TILES)
                     if not (c_ == 2 and t < CT)])
        N_HI = count([k for k in USES if k[0] in ("tc", "hT")])
        N_XN = count([(L, t) for L in range(DEPTH) for t in range(TILES)])
        N_NEW = count([(L, t) for L in range(DEPTH) for t in q_tiles(L)])
        NX = [TILES * 16, TILES * 32, TILES * 32 + len(GROUPS[1]) * 16]
        DOTS = 2

        def stacked(eng, n):
            for m in range(max(n - NSLOT + 1, 0), n + 1):
                eng.wait_ge(stack_in[m % NSLOT], STACKED[m])

        def freed(eng, use):
            n = USE[use] - 8
            if n >= 0:
                k = USES[n]
                if k[0] in BY_DVE:
                    eng.wait_ge(free_dve, N_FREE_DVE[k])
                else:
                    eng.wait_ge(free_act, N_FREE_ACT[k])

        def tokens(g):
            return slice(GROUPS[g][0] * P, (GROUPS[g][-1] + 1) * P)

        def qcols(L):
            return slice(0 if L < DEPTH - 1 else NCTX, NTOK)

        def bcast(ap, n):
            return ap.unsqueeze(2).broadcast_to((ap.shape[0], ap.shape[1], n))

        def across(ap, m):
            return ap.unsqueeze(1).broadcast_to((ap.shape[0], m, ap.shape[1]))

        block = stack.enter_context(nc.Block())

        @block.sync
        def _(sp):
            def x_rows(L, t):
                if L:
                    return x_mid[t * P:(t + 1) * P, :]
                return ctx_in[0, t * P:(t + 1) * P, :] if t < CT else x[0, (t - CT) * P:(t - CT + 1) * P, :]

            def load_piece(p):
                n = PIECE[p]
                kind, L, a, kp = p
                if n >= NRAW:
                    q = PIECES[n - NRAW]
                    if q[0] == "ada" and q in N_ADA:
                        sp.wait_ge(ada_used, N_ADA[q])
                    elif q[0] == "ada":
                        sp.wait_ge(filled, USE[q[:3]] + 1)
                    else:
                        sp.wait_ge(w_lo, N_SLICE[last_slice(q)])
                slot = w_raw[:, n % NRAW]
                done = raw_in[n % NRAW]
                if kind == "ada":
                    if kp == 0:
                        if a >= 2:
                            sp.wait_ge(filled, USE["ada", L, a - 2] + 1)
                        sp.dma_start(b_row[:, a % 2, :], b_ada[L:L + 1, a * 512:(a + 1) * 512]).then_inc(bias_in, 16)
                    src = w_ada[L, kp * 256:(kp + 1) * 256, a * 512:(a + 1) * 512]
                    sp.dma_start(slot, src.rearrange("(k p) n -> p k n", k=2)).then_inc(done, 16)
                elif kind == "in":
                    at = 0
                    for i, (c0, w) in enumerate(CHUNKS[a]):
                        src = w_in[L, kp * 256:(kp + 1) * 256, c0:c0 + w].rearrange("(k p) n -> p k n", k=2)
                        sp.dma_start(slot[:, :, at:at + w], src).then_inc(done, 16)
                        at += w
                elif kind == "uq":
                    sp.dma_start(slot[0:UQ].rearrange("p a n -> p (a n)")[:, 0:576],
                                 w_uq[L, a * UQ:(a + 1) * UQ, :]).then_inc(done, 16)
                elif kind == "ukv":
                    sp.dma_start(slot.rearrange("p a n -> p (a n)")[:, 0:768], w_ukv[L]).then_inc(done, 16)
                else:
                    src = w_out[L, kp * 256:(kp + 1) * 256, a * 512:(a + 1) * 512]
                    sp.dma_start(slot, src.rearrange("(k p) n -> p k n", k=2)).then_inc(done, 16)

            sp.dma_start(c_rows[0:8, :], c.rearrange("a (k p) -> (a k) p", p=P)).then_inc(c_in, 16)
            sp.dma_start(c_rows[8:16, :], c_ctx.rearrange("(k p) -> k p", p=P)).then_inc(c_in, 16)
            for p in PIECES[:NRAW]:
                load_piece(p)
            def load_consts():
                sp.dma_start(r64[:].rearrange("p s t n -> p (s t) n"), rope64.rearrange("s (t p) n -> p (s t) n", p=P)).then_inc(consts_in, 16)
                sp.dma_start(r32[:].rearrange("p s t n -> p (s t) n"), rope32.rearrange("s (t p) n -> p (s t) n", p=P)).then_inc(consts_in, 16)
                sp.dma_start(rt[64:128, :], rope_t).then_inc(consts_in, 16)
                for L in range(DEPTH):
                    sp.dma_start(gains[:, L, 0, :], gqa_q_g[L].partition_broadcast(P)).then_inc(consts_in, 16)
                    sp.dma_start(gains[:, L, 1, :], gqa_k_g[L].partition_broadcast(P)).then_inc(consts_in, 16)
                    sp.dma_start(mgain[:, L, 0:RANK_Q], mla_q_g[L].partition_broadcast(P)).then_inc(consts_in, 16)
                    sp.dma_start(mgain[:, L, RANK_Q:], mla_kv_g[L].partition_broadcast(P)).then_inc(consts_in, 16)
                    sp.dma_start(sgain[:, L, :], subln_g[L].partition_broadcast(P)).then_inc(consts_in, 16)
                    for i in range(4):
                        sp.dma_start(lam_in[:, L, i, :], lam_vec[i][L].partition_broadcast(P)).then_inc(consts_in, 16)

            def move(dst, src):
                return sp.dma_start(dst.bitcast(F32), src.bitcast(F32))

            def load_unit(L, u):
                n = UN[L, u]
                s = slots[:, n % NSLOT]
                done = stack_in[n % NSLOT]
                if n >= NSLOT:
                    sp.wait_ge(p_used, UNIT_END[n - NSLOT])
                q = qcols(L)
                if family(u) == "gqa":
                    r = 64 * (u % 2)
                    k = 64 * (u // 3)
                    first = max(v for v in (0, 2, 4) if v <= u)
                    sp.wait_ge(split_lo, N_SPLIT[L, first])
                    rows = [(0, 0, 64, 0, r, q), (0, 64, 128, 1, r, q), (1, 0, 64, 0, r, q),
                            (2, 0, 64, 2, k, slice(0, NTOK)), (2, 64, 128, 2, k, slice(0, NTOK)),
                            (3, 0, 64, 3, k, slice(0, NTOK))]
                    one = s[64:65, 3, :]
                    w = 64
                elif family(u) == "diff":
                    r = k = 32 * ((u - 6) % 4)
                    sp.wait_ge(split_lo, N_SPLIT[L, 6 if u < 10 else 10])
                    rows = [(0, 0, 32, 0, r, q), (0, 32, 64, 1, r, q), (0, 64, 96, 0, r, q),
                            (2, 0, 32, 2, k, slice(0, NTOK)), (2, 32, 64, 2, k, slice(0, NTOK)),
                            (2, 64, 96, 3, k, slice(0, NTOK))]
                    one = s[96:97, 2, :]
                    w = 32
                else:
                    sp.wait_ge(free_dve, N_FREE_DVE[compressed_blocks(L)[-1]])
                    rows = []
                    for f, j in ((2, 6), (3, 7)):
                        move(s[64:96, f, :], cmp_t[64:96, j, :]).then_inc(done, 16)
                    one = s[96:97, 2, :]
                    w = 0
                for f, r0, r1, part, src, cols in rows:
                    move(s[r0:r1, f, cols], parts[src:src + w, part, cols]).then_inc(done, 16)
                if n == 0:
                    sp.wait_ge(dve_const, 1)
                move(one.rearrange("o (t n) -> o t n", n=P), across(ones_r[:], TILES)).then_inc(done, 16)

            def load_maxrow(L, u):
                n = UN[L, u]
                sp.wait_ge(mrow_ready, n + 1)
                nt = len(q_tiles(L))
                f = 1 if family(u) == "gqa" else 0
                row = ROW[family(u)]
                dst = slots[row:row + 1, n % NSLOT, f, qcols(L)].rearrange("o (t n) -> o t n", t=nt)
                move(dst, m_row[0:nt, n % 2, :]).then_inc(mrow_in[n % NSLOT], 16)

            for L in range(DEPTH):
                for p in [p for p in PIECES if p[1] == L and p[0] != "out"][NRAW:]:
                    load_piece(p)
                    n = PIECE[p]
                    if L == 0 and n % 3 == 2 and 5 <= n < 5 + 3 * TILES:
                        t = n // 3 - 1
                        sp.dma_start(xb[:, t, :], x_rows(0, t)).then_inc(x_in, 16)
                    if p == ("ada", 0, 5, KD // 2 - 1):
                        load_consts()
                sp.wait_ge(filled, USE["z", L, CHUNK_ORDER[-1], TILES - 1] + 1)
                for i in STEPS:
                    if 0 <= i + 3 < NUNIT:
                        load_unit(L, i + 3)
                    if 0 <= i + 1 < NUNIT:
                        load_maxrow(L, i + 1)
                    if i == 16:
                        for p in [("out", L, 0, kp) for kp in range(NRAW)]:
                            load_piece(p)
                gs = range(2) if L < DEPTH - 1 else [1]
                sp.wait_ge(filled, USE["hT", L, list(gs)[0], 0] + 1)
                if L:
                    sp.wait_ge(stored, 16 * TILES)
                for t in q_tiles(L):
                    sp.dma_start(xb[:, t, :], x_rows(L, t)).then_inc(x_in, 16)
                sp.wait_ge(filled, USE["hT", L, 1, KD - 1] + 1)
                sp.dma_start(ends[:, 2, :], ln_g[L].partition_broadcast(P)).then_inc(ends_in, 16)
                sp.dma_start(ends[:, 3, :], ln_b[L].partition_broadcast(P)).then_inc(ends_in, 16)
                for p in [p for p in PIECES if p[0] == "out" and p[1] == L][NRAW:]:
                    load_piece(p)
                if L < DEPTH - 1:
                    for p in [p for p in PIECES if p[1] == L + 1][:NRAW]:
                        load_piece(p)
            sp.wait_ge(stored, 16 * len(N_NEW))

        N_CONST = 16 * (3 + DEPTH * 9)

        def slice_used(eng, s):
            n = RING_AT[s] - NW
            if n >= 0:
                q = RING_SLICES[n]
                if q in N_USED:
                    eng.wait_ge(w_used, N_USED[q])
                elif q[0] == "in":
                    eng.wait_ge(filled, USE["z", q[1], q[2], TILES - 1] + 1)
                else:
                    eng.wait_ge(filled, USE["y", q[1], 0, TILES - 1] + 1)

        def late_slice(k):
            area, at = (cmp_t, k) if k < 6 else (parts, k - 6)
            flat = area[:].rearrange("p a n -> p (a n)")
            return [flat[:, (2 * at + i) * 512:(2 * at + i + 1) * 512] for i in range(2)]

        def w_views(s):
            kind, L, a, k = s
            raw = w_raw[:, PIECE[piece_of(s)] % NRAW]
            if kind == "out" and a == 1:
                hi, lo = late_slice(k)
                return [(raw[:, k % 2, :], hi, lo)]
            if kind in ("in", "out"):
                w = WIDTH[a] if kind == "in" else 512
                slot = RING_AT[s] % NW
                return [(raw[:, k % 2, 0:w], w_split[:, slot, 0, 0:w], w_split[:, slot, 1, 0:w])]
            flat = raw.rearrange("p a n -> p (a n)")
            if kind == "ukv":
                return [(flat[:, 0:768], ukv[:, 0, :], ukv[:, 1, :])]
            src = flat[0:UQ, 0:576].rearrange("p (h n) -> p h n", h=6)
            hi, lo = (uq[:, i, a, :].rearrange("p (h n) -> p h n", h=6) for i in range(2))
            views = [(src, hi[:, :, 0:96], lo[:, :, 0:96])]
            for ab in range(2):
                def half_of(ap, at, z):
                    return ap[:, :, at:at + 32].rearrange("p h (r b q) -> p h r b q", r=2, b=2)[:, :, :, z, :]
                views.append((half_of(src, 64, 1 - ab), half_of(hi, 96, ab), half_of(lo, 96, ab)))
            return views

        def w_slot_ready(eng, s):
            if s[0] == "out" and s[2] == 1:
                eng.wait_ge(ring_filled, N_RINGB[s[1], NUNIT - 1, "mla", mla_parts(s[1])[-1]])
                stacked(eng, UN[s[1], NUNIT - 1])
            elif s[0] in ("in", "out"):
                slice_used(eng, s)
            if s[0] == "uq":
                eng.wait_ge(filled, USE["z", s[1], CHUNK_ORDER[-1], TILES - 1] + 1)
            if s[0] == "out" and s[2] == 0 and s[3] < NW:
                eng.wait_ge(ring_filled, N_RINGB[s[1], NUNIT - 1, "mla", mla_parts(s[1])[-1]])

        PASSES = {"gqa": [(2, 0, 128), (3, 1, 65)], "diff": [(2, 0, 97)], "mla": [(2, 0, 97), (2, 1, 96), (3, 0, 96)]}
        MAXROWS = {"gqa": 128, "diff": 96, "mla": 96}
        lat = slice(NCTX, NTOK)

        def max_bank(m, u):
            return 5 if u < 2 and m % 2 else 3

        probs = area_z
        NP = 3

        @block.tensor
        def _(pe):
            def three(dst, a, b, first=True, last=True):
                nc.tensor.matmul(dst, a[0], b[0], start=first, stop=False)
                nc.tensor.matmul(dst, a[0], b[1], start=False, stop=False)
                return nc.tensor.matmul(dst, a[1], b[0], start=False, stop=last)

            def ada(L):
                for ch in range(6):
                    use = ("ada", L, ch)
                    freed(pe, use)
                    pe.wait_ge(bias_in, 16 * (6 * L + ch + 1))
                    nc.tensor.matmul(bank(use)[0:2, :], ones[0:1, 0:2], b_row[:, ch % 2, :], start=True, stop=False)
                    for kp in range(KD // 2):
                        p = ("ada", L, ch, kp)
                        slot = PIECE[p] % NRAW
                        pe.wait_ge(raw_in[slot], RAW_VALUE[p])
                        for k in range(2):
                            mm = nc.tensor.matmul(bank(use)[0:2, :], c_silu[:, 2 * kp + k::8], w_raw[:, slot, k, :],
                                                  start=False, stop=(kp == KD // 2 - 1 and k == 1))
                        mm.then_inc(ada_used if p in N_ADA else filled, 1)
                use = ("adaT", L)
                freed(pe, use)
                pe.wait_ge(free_act, N_FREE_ACT["ada", L, 3])
                for j in range(16):
                    mm = nc.tensor.transpose(bank(use)[:, 2 * j:2 * j + 2], ada_row[:, j * P:(j + 1) * P], ident[0:2, 0:2])
                mm.then_inc(filled, 1)

            def turn_x(L):
                for g in range(2):
                    for t in GROUPS[g]:
                        pe.wait_ge(xn_ready, N_XN[L, t])
                    for k in range(KD):
                        use = ("xT", L, g, k)
                        freed(pe, use)
                        for i, t in enumerate(GROUPS[g]):
                            mm = nc.tensor.transpose(bank(use)[:, i * P:(i + 1) * P], xb[:, t, k * P:(k + 1) * P], ident[:])
                        mm.then_inc(filled, 1)

            def project(L, c_):
                tiles = chunk_tiles(L, c_)
                for k in range(KD):
                    s = ("in", L, c_, k)
                    slot = RING_AT[s] % NW
                    pe.wait_ge(w_lo, N_SLICE[s])
                    for t in tiles:
                        use = ("z", L, c_, t)
                        if k == 0:
                            freed(pe, use)
                        if c_ == CHUNK_ORDER[0]:
                            pe.wait_ge(h_ready, N_H[L, int(t >= CT), k])
                        a, b = chunk_cols(L, c_, t)
                        mm = three(bank(use)[:, a:b], [h_t[:, i, k, t * P:(t + 1) * P] for i in range(2)],
                                   [w_split[:, slot, i, a:b] for i in range(2)], k == 0, k == KD - 1)
                        if k == KD - 1:
                            mm.then_inc(filled, 1)
                    if k < KD - 1:
                        mm.then_inc(w_used, 1)

            def turn_blocks(L, first):
                for use in transposed_blocks(L, first):
                    _, _, b, g = use
                    freed(pe, use)
                    for i, t in enumerate(GROUPS[g]):
                        if (L, first // 2, t) in N_Z:
                            pe.wait_ge(z_ready, N_Z[L, first // 2, t])
                        else:
                            pe.wait_ge(free_act, N_FREE_ACT["z", L, first // 2, t])
                        mm = nc.tensor.transpose(bank(use)[:, i * P:(i + 1) * P],
                                                 area_z[:, t, (b - first) * P:(b - first + 1) * P], ident[:])
                    mm.then_inc(filled, 1)

            def turn_compressed(L):
                at = [(0, 96), (96, 192), (192, 320), (256, 352)]
                for use in compressed_blocks(L):
                    _, _, j, g = use
                    a, b = at[j]
                    freed(pe, use)
                    for i, t in enumerate(GROUPS[g]):
                        pe.wait_ge(z_ready, N_Z[L, 3, t])
                        mm = nc.tensor.transpose(bank(use)[0:b - a, i * P:(i + 1) * P], area_z[:, t, a:b], ident[:])
                    mm.then_inc(filled, 1)

            def mla_values(L):
                pe.wait_ge(w_lo, N_SLICE["ukv", L, 0, 0])
                for t in range(TILES):
                    use = ("vm", L, t)
                    freed(pe, use)
                    pe.wait_ge(free_dve, N_FREE_DVE["tc", L, 2, int(t >= CT)])
                    v = [ukv[:, i, :].rearrange("p (h n) -> p h n", h=6)[:, :, 64:128] for i in range(2)]
                    three(bank(use)[:, 0:384], [cmp_t[:, 4 + i, t * P:(t + 1) * P] for i in range(2)], v).then_inc(filled, 1)

            def ring_ready(r):
                if r >= NP:
                    k = RING[r - NP]
                    if k in N_P:
                        pe.wait_ge(p_ready, N_P[k])
                    else:
                        pe.wait_ge(ring_free, N_RING_FREE[k])

            def mla_head(L, u):
                h = u - 14
                pe.wait_ge(w_lo, N_SLICE["uq", L, 1, 0])
                for part in mla_parts(L):
                    r = N_RINGB[L, u, "mla", part] - 1
                    ring_ready(r)
                    what, g = part
                    n = len(GROUPS[g]) * P
                    dst = banks[:, r % NP, 0:n]
                    if what == "q":
                        for j in range(2):
                            mm = three(dst, [uq[:, i, j, h * P:(h + 1) * P] for i in range(2)],
                                       [cmp_t[0:UQ, 2 * i + j, tokens(g)] for i in range(2)], j == 0, j == 1)
                    else:
                        mm = three(dst, [ukv[:, i, h * P:(h + 1) * P] for i in range(2)],
                                   [cmp_t[:, 4 + i, tokens(g)] for i in range(2)])
                    mm.then_inc(ring_filled, 1)

            def max_tile(L, u, t):
                n = UN[L, u]
                m = N_MAX[L, u, t]
                if t == q_tiles(L)[0]:
                    stacked(pe, n)
                    if family(u) == "mla":
                        pe.wait_ge(mla_lo, N_MLA[L, u])
                ago = 2 if u < 2 and m - 1 > N_MAX[L, 0, q_tiles(L)[0]] else 1
                if m > ago:
                    pe.wait_ge(max_read, m - ago)
                b0 = max_bank(m, u)
                s, rows = slots[:, n % NSLOT], MAXROWS[family(u)]
                q = s[0:rows, 0, t * P:(t + 1) * P]
                if t < CT:
                    mm = nc.tensor.matmul(banks[:, b0, 0:NCTX], q, s[0:rows, 2, 0:NCTX], start=True, stop=True)
                else:
                    for i in range(2):
                        mm = nc.tensor.matmul(banks[:, b0 + i, 0:384], q, s[0:rows, 2, i * 384:(i + 1) * 384],
                                              start=True, stop=True)
                mm.then_inc(max_filled, 1)

            def turn_max(L, u):
                n = UN[L, u]
                tiles = q_tiles(L)
                pe.wait_ge(max_read, N_MAX[L, u, tiles[-1]])
                if n >= 3:
                    pe.wait_ge(o_read, n - 2)
                nc.tensor.transpose(banks[0:len(tiles), 7, 0:P], negmax[:, n % 2, tiles[0]:TILES], ident[:]).then_inc(mt_filled, 1)

            def scores(L, u, step):
                n = UN[L, u]
                r = N_RINGB[L, u, "s", step] - 1
                ring_ready(r)
                if step == 0:
                    pe.wait_ge(mrow_in[n % NSLOT], 16 * (n // NSLOT + 1))
                s = slots[:, n % NSLOT]
                todo = [(kt, slice(0, NCTX), kt * NCTX) for kt in range(CT)] if step == "ctx" else [(step, lat, 0)]
                passes = PASSES[family(u)]
                for kt, cols, at in todo:
                    for i, (kf, qf, rows) in enumerate(passes):
                        mm = nc.tensor.matmul(banks[:, r % NP, at:at + cols.stop - cols.start],
                                              s[0:rows, kf, kt * P:(kt + 1) * P], s[0:rows, qf, cols],
                                              start=(i == 0), stop=(i == len(passes) - 1))
                mm.then_inc(ring_filled, 1)

            def mix(L, u, step):
                n = UN[L, u]
                e = N_P[L, u, "s", step]
                pe.wait_ge(p_ready, e)
                if step == 0 and n >= 1:
                    pe.wait_ge(o_copied, n)
                if step == "ctx" and N_CTX[L, u] > 1:
                    pe.wait_ge(ctx_copied, N_CTX[L, u] - 1)
                vh = value_head(u)
                pr = probs[:, (e - 1) % NP, :]
                if step == "ctx":
                    for kt in range(CT):
                        mm = nc.tensor.matmul(banks[0:65, 6, 0:NCTX], vals[:, kt, vh, :], pr[:, kt * NCTX:(kt + 1) * NCTX],
                                              start=(kt == 0), stop=(kt == CT - 1))
                else:
                    mm = nc.tensor.matmul(banks[0:65, 5, :], vals[:, step, vh, :], pr, start=(step == 0), stop=(step == TILES - 1))
                mm.then_inc(p_used, 1)

            def turn_output(L, u):
                n = UN[L, u]
                pe.wait_ge(o_copied, n + 1)
                if L < DEPTH - 1:
                    pe.wait_ge(ctx_copied, N_CTX[L, u])
                pe.wait_ge(mrow_ready, min(n + 3, (L + 1) * NUNIT))
                if n:
                    pe.wait_ge(o_read, n)
                for i, t in enumerate(q_tiles(L)):
                    mm = nc.tensor.transpose(banks[:, 7, i * 65:(i + 1) * 65], o_t[0:65, t * P:(t + 1) * P], ident[0:65, 0:65])
                mm.then_inc(ot_filled, 1)

            def attend(L):
                pe.wait_ge(free_act, N_FREE_ACT["vm", L, TILES - 1])
                pe.wait_ge(free_dve, N_FREE_DVE[compressed_blocks(L)[-1]])
                for i in STEPS:
                    if 14 <= i + 4 < NUNIT:
                        mla_head(L, i + 4)
                    steps = score_steps(L)
                    for j in range(9):
                        m = j - 2
                        if 0 <= i + 2 < NUNIT and 0 <= m < len(q_tiles(L)):
                            max_tile(L, i + 2, q_tiles(L)[m])
                        if 0 <= i < NUNIT and j < len(steps):
                            scores(L, i, steps[j])
                        if 0 <= i < NUNIT and 2 <= j <= len(steps) + 1:
                            mix(L, i, steps[j - 2])
                        if j == 3 and 0 <= i + 1 < NUNIT:
                            turn_max(L, i + 1)
                        if j == 5 and 0 <= i - 1:
                            turn_output(L, i - 1)

            def project_out(L):
                pe.wait_ge(gated, len([k for k in N_GATE if k[0] <= L]))
                gs = range(2) if L < DEPTH - 1 else [1]
                for g in gs:
                    for k in range(KD):
                        use = ("hT", L, g, k)
                        if USE[use] - 8 >= AFTER_ATTENTION[L]:
                            freed(pe, use)
                        for i, t in enumerate(GROUPS[g]):
                            mm = nc.tensor.transpose(bank(use)[:, i * P:(i + 1) * P], gates[:, t, k * P:(k + 1) * P], ident[:])
                        mm.then_inc(filled, 1)
                for g in gs:
                    for h in range(2):
                        use = ("gt", L, g, h)
                        freed(pe, use)
                        nc.tensor.matmul(bank(use), sel[:, 1 - g, :], gate_row[:, h * 512:(h + 1) * 512],
                                         start=True, stop=True).then_inc(filled, 1)
                for k in range(KD):
                    s = ("out", L, 0, k)
                    slot = RING_AT[s] % NW
                    pe.wait_ge(w_lo, N_SLICE[s])
                    for t in q_tiles(L):
                        use = ("y", L, 0, t)
                        if k == 0:
                            freed(pe, use)
                        pe.wait_ge(free_dve, N_FREE_DVE["hT", L, int(t >= CT), k])
                        mm = three(bank(use), [h_t[:, i, k, t * P:(t + 1) * P] for i in range(2)],
                                   [w_split[:, slot, i, :] for i in range(2)], k == 0, k == KD - 1)
                        if k == KD - 1:
                            mm.then_inc(filled, 1)
                    if k < KD - 1:
                        mm.then_inc(w_used, 1)
                for t in q_tiles(L):
                    use = ("y", L, 1, t)
                    freed(pe, use)
                    for k in range(KD):
                        pe.wait_ge(w_lo, N_SLICE["out", L, 1, k])
                        mm = three(bank(use), [h_t[:, i, k, t * P:(t + 1) * P] for i in range(2)],
                                   late_slice(k), k == 0, k == KD - 1)
                    mm.then_inc(filled, 1)

            pe.wait_ge(c_in, 32)
            pe.wait_ge(pool_const, 1)
            nc.tensor.transpose(bank(("cT", 0))[:, 0:16], c_rows, ident[0:16, 0:16]).then_inc(filled, 1)
            pe.wait_ge(free_act, N_FREE_ACT["cT", 0])
            for L in range(DEPTH):
                ada(L)
                turn_x(L)
                for c_ in CHUNK_ORDER:
                    project(L, c_)
                    if c_ in (1, 4):
                        turn_blocks(L, 0 if c_ == 1 else 4)
                turn_compressed(L)
                mla_values(L)
                attend(L)
                project_out(L)

        @block.scalar
        def _(act):
            def copy(dst, src):
                return nc.scalar.activation(dst, src, ACT.Copy)

            def split_w(s):
                act.wait_ge(raw_in[PIECE[piece_of(s)] % NRAW], RAW_VALUE[piece_of(s)])
                w_slot_ready(act, s)
                for raw, hi, lo in w_views(s):
                    op = copy(hi, raw)
                op.then_inc(w_hi, 1)

            def evacuate_ada(L):
                for ch in range(6):
                    use = ("ada", L, ch)
                    act.wait_ge(filled, USE[use] + 1)
                    dst = ada_row[:, ch * 512:(ch + 1) * 512] if ch < 4 else gate_row[:, (ch - 4) * 512:(ch - 3) * 512]
                    copy(dst, bank(use)[0:2, :]).then_inc(free_act, 1)

            def modulate(L):
                act.wait_ge(free_dve, N_FREE_DVE["adaT", L])
                for g in range(2):
                    for k in range(KD):
                        use = ("xT", L, g, k)
                        n = N_H[L, g, k]
                        n_tok = len(GROUPS[g]) * P
                        act.wait_ge(filled, USE[use] + 1)
                        if n > 2:
                            act.wait_ge(h_ready, n - 2)
                        nc.scalar.activation(area_z[:, n % 2, 0:n_tok], bank(use)[:, 0:n_tok], ACT.Identity,
                                             bias=ada_col[:, k, 1 - g:2 - g], scale=ada_col[:, 8 + k, 1 - g:2 - g]).then_inc(free_act, 1)

            def evacuate_z(L, c_):
                if c_ == CHUNK_ORDER[0]:
                    act.wait_ge(h_ready, N_H[L, 1, KD - 1])
                for t in chunk_tiles(L, c_):
                    use = ("z", L, c_, t)
                    a, b = chunk_cols(L, c_, t)
                    act.wait_ge(filled, USE[use] + 1)
                    src = bank(use)[:, a:b]
                    if c_ == 1:
                        op = copy(vals[:, t, 0:6, 0:64], src.rearrange("p (h n) -> p h n", h=6))
                    elif c_ in (4, 5):
                        op = nc.scalar.activation(gates[:, t, (c_ - 4) * 512:(c_ - 3) * 512], src, ACT.Silu)
                    else:
                        op = copy(area_z[:, t, a:b], src)
                    op.then_inc(free_act, 1)

            def compressed_hi(L):
                for use in compressed_blocks(L):
                    _, _, j, g = use
                    act.wait_ge(filled, USE[use] + 1)
                    r0, r1, hi = [(0, 96, 0), (0, 96, 1), (0, 128, 4), (64, 96, 6)][j]
                    copy(cmp_t[r0:r1, hi, tokens(g)], bank(use)[r0:r1, 0:len(GROUPS[g]) * P]).then_inc(hi_ready, 1)

            def mla_copy(L, u):
                m = N_MLA[L, u]
                if m > 2:
                    act.wait_ge(mla_lo, m - 2)
                for part in mla_parts(L):
                    r = N_RINGB[L, u, "mla", part] - 1
                    what, g = part
                    rows = P if what == "q" else 64
                    act.wait_ge(ring_filled, r + 1)
                    copy(qk_t[0:rows, 2 * (m % 2) + (what == "k"), tokens(g)],
                         banks[0:rows, r % NP, 0:len(GROUPS[g]) * P]).then_inc(ring_free, 1)

            def mla_high(L, u):
                n, m = UN[L, u], N_MLA[L, u]
                act.wait_ge(mla_roped, m)
                if n >= NSLOT:
                    act.wait_ge(p_used, UNIT_END[n - NSLOT])
                s = slots[:, n % NSLOT]
                copy(s[0:96, 0, qcols(L)], qk_t[0:96, 2 * (m % 2), qcols(L)])
                copy(s[0:64, 2, :], qk_t[0:64, 2 * (m % 2) + 1, :]).then_inc(mla_hi, 1)

            def split_block(L, u):
                n = UN[L, u]
                if n:
                    stacked(act, n - 1)
                qb, kb = blocks_of(u)
                for b in (qb, kb):
                    if b is not None:
                        for g in range(2):
                            if ("tp", L, b, g) in N_FREE_DVE:
                                act.wait_ge(free_dve, N_FREE_DVE["tp", L, b, g])
                op = copy(parts[:, 0, qcols(L)], qk_t[:, qb, qcols(L)])
                if kb is not None:
                    op = copy(parts[:, 2, :], qk_t[:, kb, :])
                op.then_inc(split_hi, 1)

            def exponent(L, u, step):
                r = N_RINGB[L, u, "s", step] - 1
                e = N_P[L, u, "s", step]
                act.wait_ge(ring_filled, r + 1)
                if e > NP:
                    act.wait_ge(p_used, e - NP)
                nc.scalar.activation(probs[:, (e - 1) % NP, :], banks[:, r % NP, :], ACT.Exp,
                                     scale=SCALE[family(u)]).then_inc(p_ready, 1)

            def copy_latents(L, u):
                n = UN[L, u]
                if n:
                    act.wait_ge(ot_filled, n)
                act.wait_ge(p_used, LATENTS_END[n])
                copy(o_t[0:65, lat], banks[0:65, 5, :]).then_inc(o_copied, 1)

            def copy_context(L, u):
                act.wait_ge(p_used, UNIT_END[UN[L, u]])
                copy(o_t[0:65, 0:NCTX], banks[0:65, 6, 0:NCTX]).then_inc(ctx_copied, 1)

            def copy_maxrow(L, u):
                n = UN[L, u]
                nt = len(q_tiles(L))
                act.wait_ge(mt_filled, n + 1)
                if n >= 2:
                    act.wait_ge(mrow_in[(n - 2) % NSLOT], 16 * ((n - 2) // NSLOT + 1))
                copy(m_row[0:nt, n % 2, :], banks[0:nt, 7, 0:P]).then_inc(mrow_ready, 1)

            def attend(L):
                act.wait_ge(lam_dots, 1)
                nc.scalar.activation(lam[:, L, 2:4], lam[:, L, 0:2], ACT.Exp).then_inc(lam_exp, 1)
                for i in STEPS:
                    if 14 <= i + 4 < NUNIT:
                        mla_copy(L, i + 4)
                    steps = score_steps(L)
                    for j in range(8):
                        if 0 <= i < NUNIT and j < len(steps):
                            exponent(L, i, steps[j])
                        if j == 0 and i >= 1 and L < DEPTH - 1:
                            copy_context(L, i - 1)
                        if j == 3 and 0 <= i + 1 < NUNIT:
                            copy_maxrow(L, i + 1)
                        if j == 1 and 14 <= i + 3 < NUNIT:
                            mla_high(L, i + 3)
                        if j == 5 and 0 < i + 4 < NUNIT and blocks_of(i + 4):
                            split_block(L, i + 4)
                    if 0 <= i < NUNIT:
                        copy_latents(L, i)

            def finish(L):
                gs = range(2) if L < DEPTH - 1 else [1]
                for g in gs:
                    for k in range(KD):
                        use = ("hT", L, g, k)
                        act.wait_ge(filled, USE[use] + 1)
                        copy(h_t[:, 0, k, tokens(g)], bank(use)[:, 0:len(GROUPS[g]) * P]).then_inc(hi_ready, 1)
                for g in gs:
                    for h in range(2):
                        use = ("gt", L, g, h)
                        act.wait_ge(filled, USE[use] + 1)
                        copy(ends[:, g, h * 512:(h + 1) * 512], bank(use)).then_inc(free_act, 1)
                for s in [s for s in SLICES if s[0] == "out" and s[1] == L]:
                    split_w(s)
                for t in q_tiles(L):
                    act.wait_ge(x_new, N_NEW[L, t])
                    dst = x_mid[t * P:(t + 1) * P, :] if L < DEPTH - 1 else out[0, (t - CT) * P:(t - CT + 1) * P, :]
                    act.dma_start(dst, xb[:, t, :]).then_inc(stored, 16)

            act.wait_ge(filled, 1)
            nc.scalar.activation(c_silu[:], bank(("cT", 0))[:, 0:16], ACT.Silu).then_inc(free_act, 1)
            for L in range(DEPTH):
                evacuate_ada(L)
                chunks = [[("in", L, c_, k) for k in range(KD)] for c_ in CHUNK_ORDER]
                for s in chunks[0][:NW]:
                    split_w(s)
                modulate(L)
                for s in chunks[0][NW:]:
                    split_w(s)
                for n, c_ in enumerate(CHUNK_ORDER):
                    if n + 1 < len(chunks):
                        for s in chunks[n + 1][:2]:
                            split_w(s)
                    evacuate_z(L, c_)
                    if c_ == 3:
                        split_block(L, 0)
                    if n + 1 < len(chunks):
                        for s in chunks[n + 1][2:]:
                            split_w(s)
                split_w(("ukv", L, 0, 0))
                for j in range(2):
                    split_w(("uq", L, j, 0))
                compressed_hi(L)
                for t in range(TILES):
                    use = ("vm", L, t)
                    act.wait_ge(filled, USE[use] + 1)
                    copy(vals[:, t, 6:12, 0:64], bank(use)[:, 0:384].rearrange("p (h n) -> p h n", h=6)).then_inc(free_act, 1)
                attend(L)
                finish(L)

        @block.gpsimd
        def _(pool):
            seq = [0]

            def chain(op):
                seq[0] += 1
                op.then_inc(pool_seq, 1)
                pool.wait_ge(pool_seq, seq[0])

            def split_w(s):
                pool.wait_ge(w_hi, N_SLICE[s])
                for raw, hi, lo in w_views(s):
                    op = nc.gpsimd.tensor_tensor(lo, raw, hi.bitcast(F32), ALU.subtract)
                op.then_inc(w_lo, 1)

            def root(key, cols):
                pool.wait_ge(var_ready, N_ROOT[key])
                nc.gpsimd.tensor_tensor(rstd[:, cols], var[:, cols], half[:, cols], ALU.pow).then_inc(root_ready, 1)

            def gate(L, u):
                n = UN[L, u]
                ts = q_tiles(L)
                c0 = gate_column(u)
                g = gates[:, ts[0]:TILES, c0:c0 + 64]
                if (L, u) in N_NORMED:
                    pool.wait_ge(normed, N_NORMED[L, u])
                else:
                    pool.wait_ge(o_read, n + 1)
                nc.gpsimd.tensor_tensor(g, g, o_v[:, n % 2, ts[0]:TILES, :], ALU.mult).then_inc(gated, 1)

            def split_block(L, u):
                pool.wait_ge(split_hi, N_SPLIT[L, u])
                qb, kb = blocks_of(u)
                op = nc.gpsimd.tensor_tensor(parts[:, 1, qcols(L)], qk_t[:, qb, qcols(L)],
                                             parts[:, 0, qcols(L)].bitcast(F32), ALU.subtract)
                if kb is not None:
                    op = nc.gpsimd.tensor_tensor(parts[:, 3, :], qk_t[:, kb, :], parts[:, 2, :].bitcast(F32), ALU.subtract)
                op.then_inc(split_lo, 1)

            nc.gpsimd.memset(half[:], -0.5)
            nc.gpsimd.memset(ones[:], 1.0)
            nc.gpsimd.memset(vals[:, :, :, 64:65], 1.0)
            nc.gpsimd.memset(sel[:], 0.0)
            chain(nc.gpsimd.memset(ident[:], 0.0))
            nc.gpsimd.affine_select(out=sel[:], in_=sel[:], compare_op=ALU.not_equal, fill=1.0, base=0,
                                    pattern=[[-1, 2], [0, P]], channel_multiplier=1)
            nc.gpsimd.affine_select(out=ident[:], in_=ident[:], compare_op=ALU.not_equal, fill=1.0, base=0,
                                    pattern=[[-1, P]], channel_multiplier=1).then_inc(pool_const, 1)
            for L in range(DEPTH):
                for t in range(TILES):
                    root(("ln", L, t), slice(t, t + 1))
                chunks = [[("in", L, c_, k) for k in range(KD)] for c_ in CHUNK_ORDER]
                for s in chunks[0]:
                    split_w(s)
                for n, c_ in enumerate(CHUNK_ORDER):
                    for k in range(KD):
                        if n + 1 < len(chunks):
                            split_w(chunks[n + 1][k])
                        if k >= 2 and c_ == 0:
                            root(("gqa", L, k - 2), slice(8 * (k - 2), 8 * (k - 1)))
                        if k == 1 and c_ == 3:
                            split_block(L, 0)
                        if k >= 2 and c_ == 3:
                            root(("mla", L, k - 2), slice(8 * (k - 2), 8 * (k - 2) + 2))
                split_w(("ukv", L, 0, 0))
                for j in range(2):
                    split_w(("uq", L, j, 0))
                for i in STEPS:
                    if (L, i - 2) in N_NORMED:
                        gate(L, i - 2)
                    if (L, i - 1) in N_NORMED:
                        root(("diff", L, i - 1), slice(0, TILES))
                    elif (L, i - 1) in N_GATE:
                        gate(L, i - 1)
                    if 0 < i + 4 < NUNIT and blocks_of(i + 4):
                        split_block(L, i + 4)
                out_slices = [s for s in SLICES if s[0] == "out" and s[1] == L]
                for s in out_slices:
                    split_w(s)
                ts = q_tiles(L)
                pool.wait_ge(ends_in, 32 * (L + 1))
                for n, t in enumerate(ts + [None]):
                    if t is not None:
                        root(("out", L, t), slice(t, t + 1))
                    if n:
                        v = xb[:, ts[n - 1], :]
                        pool.wait_ge(scaled, N_NEW[L, ts[n - 1]])
                        nc.gpsimd.tensor_tensor(v, v, ends[:, 3, :], ALU.add).then_inc(x_new, 1)

        @block.vector
        def _(dve):
            seq = [0]

            def chain(op):
                seq[0] += 1
                op.then_inc(dve_seq, 1)
                dve.wait_ge(dve_seq, seq[0])

            def layer_stats(x_tile, t, key):
                for i in range(2):
                    op = nc.vector.bn_stats(stats[:, t, i, :], x_tile[:, i * 512:(i + 1) * 512])
                chain(op)
                chain(nc.vector.bn_aggr(mean_var[:, t, :], stats[:, t].rearrange("p a b -> p (a b)")))
                nc.vector.tensor_scalar(var[:, t:t + 1], mean_var[:, t, 1:2], EPS, None, ALU.add).then_inc(var_ready, 1)

            def normalize(x_tile, t, key):
                dve.wait_ge(root_ready, N_ROOT[key])
                return nc.vector.tensor_scalar(x_tile, x_tile, mean_var[:, t, 0:1], rstd[:, t:t + 1], ALU.subtract, ALU.mult)

            def rope(v, heads, quarter, table, t):
                width = 4 * quarter
                n = heads * width
                a, b = scr[:, 0, 0:n], scr[:, 1, 0:n]

                def three_d(ap):
                    return ap.rearrange("p (h n) -> p h n", h=heads)

                def half_of(ap, z):
                    return ap.rearrange("p (h r b q) -> p h r b q", h=heads, r=2, b=2)[:, :, :, z, :]

                tab = table[:, :, t - CT, :]
                nc.vector.tensor_tensor(three_d(a), three_d(v), across(tab[:, 0, :], heads), ALU.mult)
                for z in range(2):
                    s = tab[:, 1, :].rearrange("p (r b q) -> p r b q", r=2, b=2)[:, :, z, :]
                    s = s.unsqueeze(1).broadcast_to((P, heads, 2, quarter))
                    op = nc.vector.tensor_tensor(half_of(b, z), half_of(v, 1 - z), s, ALU.mult)
                chain(op)
                return nc.vector.tensor_tensor(v, a, b, ALU.add)

            def gqa_rows(L):
                def heads_of(t):
                    return (4, 8) if L == DEPTH - 1 and t < CT else (0, 8)
                for t in range(TILES):
                    h0, h1 = heads_of(t)
                    z = area_z[:, t, 64 * h0:64 * h1]
                    sq = scr[:, t % 2, 0:64 * (h1 - h0)]
                    dve.wait_ge(free_act, N_FREE_ACT["z", L, 0, t])
                    chain(nc.vector.tensor_tensor(sq, z, z, ALU.mult))
                    v = var[:, 8 * t + h0:8 * t + h1]
                    chain(nc.vector.tensor_reduce(v, sq.rearrange("p (h n) -> p h n", n=64), AX.X, ALU.add))
                    if h0:
                        nc.vector.memset(var[:, 8 * t:8 * t + h0], 1.0)
                    nc.vector.tensor_scalar(v, v, 1.0 / 64, EPS, ALU.mult, ALU.add).then_inc(var_ready, 1)
                for t in range(TILES):
                    h0, h1 = heads_of(t)
                    z = area_z[:, t, 64 * h0:64 * h1]
                    z3 = z.rearrange("p (h n) -> p h n", n=64)
                    dve.wait_ge(root_ready, N_ROOT["gqa", L, t])
                    chain(nc.vector.tensor_tensor(z3, z3, bcast(rstd[:, 8 * t + h0:8 * t + h1], 64), ALU.mult))
                    nq = 6 - h0
                    nc.vector.tensor_tensor(z3[:, 0:nq, :], z3[:, 0:nq, :], across(gains[:, L, 0, :], nq), ALU.mult)
                    op = nc.vector.tensor_tensor(z3[:, nq:, :], z3[:, nq:, :], across(gains[:, L, 1, :], 2), ALU.mult)
                    if t >= CT:
                        chain(op)
                        op = rope(z, 8, 16, r64, t)
                    op.then_inc(z_ready, 1)
                    dve.wait_ge(z_ready, N_Z[L, 0, t])

            def diff_rows(L):
                for t in GROUPS[1]:
                    dve.wait_ge(free_act, N_FREE_ACT["z", L, 2, t])
                    rope(area_z[:, t, :], 16, 8, r32, t).then_inc(z_ready, 1)
                    dve.wait_ge(z_ready, N_Z[L, 2, t])

            def mla_rows(L):
                def segments(t):
                    kv = (RANK_Q, RANK_Q + RANK_KV, 1)
                    return [kv] if L == DEPTH - 1 and t < CT else [(0, RANK_Q, 0), kv]
                for t in range(TILES):
                    dve.wait_ge(free_act, N_FREE_ACT["z", L, 3, t])
                    if len(segments(t)) == 1:
                        nc.vector.memset(var[:, 8 * t:8 * t + 1], 1.0)
                    for a, b, i in segments(t):
                        v = var[:, 8 * t + i:8 * t + i + 1]
                        z = area_z[:, t, a:b]
                        chain(nc.vector.tensor_tensor_reduce(out=scr[:, 0, 0:b - a], in0=z, in1=z, scale=1.0, scalar=0.0,
                                                             op0=ALU.mult, op1=ALU.add, accum_out=v))
                        op = nc.vector.tensor_scalar(v, v, 1.0 / (b - a), EPS, ALU.mult, ALU.add)
                    op.then_inc(var_ready, 1)
                for t in range(TILES):
                    dve.wait_ge(root_ready, N_ROOT["mla", L, t])
                    for a, b, i in segments(t):
                        z = area_z[:, t, a:b]
                        op = nc.vector.scalar_tensor_tensor(out=z, in0=z, scalar=rstd[:, 8 * t + i:8 * t + i + 1],
                                                            in1=mgain[:, L, a:b], op0=ALU.mult, op1=ALU.mult)
                    if t >= CT:
                        op = rope(area_z[:, t, 320:352], 1, 8, r32, t)
                    op.then_inc(z_ready, 1)
                    dve.wait_ge(z_ready, N_Z[L, 3, t])

            def copy_blocks(L, first):
                for use in transposed_blocks(L, first):
                    _, _, b, g = use
                    dve.wait_ge(filled, USE[use] + 1)
                    nc.vector.tensor_copy(qk_t[:, b, tokens(g)], bank(use)[:, 0:len(GROUPS[g]) * P]).then_inc(free_dve, 1)

            def compressed_lo(L):
                for use in compressed_blocks(L):
                    _, _, j, g = use
                    dve.wait_ge(hi_ready, N_HI[use])
                    r0, r1, hi, lo = [(0, 96, 0, 2), (0, 96, 1, 3), (0, 128, 4, 5), (64, 96, 6, 7)][j]
                    nc.vector.tensor_tensor(cmp_t[r0:r1, lo, tokens(g)], bank(use)[r0:r1, 0:len(GROUPS[g]) * P],
                                            cmp_t[r0:r1, hi, tokens(g)].bitcast(F32), ALU.subtract).then_inc(free_dve, 1)

            def reduce_max(L, u, t):
                m = N_MAX[L, u, t]
                n = UN[L, u]
                dve.wait_ge(max_filled, m)
                if t == q_tiles(L)[0] and n >= 2:
                    dve.wait_ge(mt_filled, n - 1)
                b0 = max_bank(m, u)
                src = banks[:, b0, 0:NCTX] if t < CT else banks[:, b0:b0 + 2, 0:384]
                nc.vector.tensor_reduce(negmax[:, n % 2, t:t + 1], src, AX.X if t < CT else AX.XY, ALU.max,
                                        negate=True).then_inc(max_read, 1)

            def mla_rope(L, u):
                m = N_MLA[L, u]
                q = qk_t[:, 2 * (m % 2), lat]
                dve.wait_ge(ring_free, N_RING_FREE[L, u, "mla", mla_parts(L)[-1]])
                nc.vector.tensor_tensor(scr[64:96, 0, :], q[64:96], rt[64:96, :], ALU.mult)
                chain(nc.vector.tensor_tensor(scr[64:96, 1, :], q[96:128], rt[96:128, :], ALU.mult))
                nc.vector.tensor_tensor(q[64:96], scr[64:96, 0, :], scr[64:96, 1, :], ALU.add).then_inc(mla_roped, 1)
                dve.wait_ge(mla_roped, m)

            def mla_low(L, u):
                n, m = UN[L, u], N_MLA[L, u]
                s = slots[:, n % NSLOT]
                dve.wait_ge(mla_hi, m)
                nc.vector.tensor_tensor(s[0:96, 1, qcols(L)], qk_t[0:96, 2 * (m % 2), qcols(L)],
                                        s[0:96, 0, qcols(L)].bitcast(F32), ALU.subtract)
                nc.vector.tensor_tensor(s[0:64, 3, :], qk_t[0:64, 2 * (m % 2) + 1, :],
                                        s[0:64, 2, :].bitcast(F32), ALU.subtract).then_inc(mla_lo, 1)

            def output_rows(L, u):
                n = UN[L, u]
                ts = q_tiles(L)
                nt = len(ts)
                src = banks[:, 7, 0:65 * nt].rearrange("p (t n) -> p t n", n=65)
                o = o_v[:, n % 2, ts[0]:TILES, :]
                dve.wait_ge(ot_filled, n + 1)
                chain(nc.vector.reciprocal(rec[:, 0:nt], src[:, :, 64]))
                if n >= 2 and UNITS[n - 2] in N_GATE:
                    dve.wait_ge(gated, N_GATE[UNITS[n - 2]])
                op = nc.vector.tensor_tensor(o, src[:, :, 0:64], bcast(rec[:, 0:nt], 64), ALU.mult)
                op.then_inc(o_read, 1)
                dve.wait_ge(o_read, n + 1)
                if (L, u) in N_NORMED:
                    other = o_v[:, 1 - n % 2, ts[0]:TILES, :]
                    sq = scr[:, 0, 0:64 * nt].rearrange("p (t n) -> p t n", n=64)
                    chain(nc.vector.scalar_tensor_tensor(out=o, in0=o, scalar=lam[:, L, 0:1], in1=other, op0=ALU.mult, op1=ALU.add))
                    chain(nc.vector.tensor_tensor(sq, o, o, ALU.mult))
                    chain(nc.vector.tensor_reduce(var[:, ts[0]:TILES], sq, AX.X, ALU.add))
                    nc.vector.tensor_scalar(var[:, ts[0]:TILES], var[:, ts[0]:TILES], 1.0 / 64, EPS,
                                            ALU.mult, ALU.add).then_inc(var_ready, 1)

            def diff_norm(L, u):
                ts = q_tiles(L)
                o = o_v[:, UN[L, u] % 2, ts[0]:TILES, :]
                dve.wait_ge(root_ready, N_ROOT["diff", L, u])
                chain(nc.vector.tensor_tensor(o, o, bcast(rstd[:, ts[0]:TILES], 64), ALU.mult))
                nc.vector.tensor_tensor(o, o, across(sgain[:, L, :], len(ts)), ALU.mult).then_inc(normed, 1)

            def attend(L):
                lam_init = 0.8 - 0.6 * math.exp(-0.3 * L)
                dve.wait_ge(lam_exp, L + 1)
                nc.vector.scalar_tensor_tensor(out=lam[:, L, 0:1], in0=lam[:, L, 3:4], scalar=-lam_init, in1=lam[:, L, 2:3],
                                               op0=ALU.add, op1=ALU.subtract)
                chain(nc.vector.tensor_scalar(sgain[:, L, :], sgain[:, L, :], 1.0 - lam_init, None, ALU.mult))
                for i in STEPS:
                    ts = q_tiles(L) if 0 <= i + 2 < NUNIT else []
                    for t in ts[:2]:
                        reduce_max(L, i + 2, t)
                    if (L, i - 2) in N_NORMED:
                        diff_norm(L, i - 2)
                    for t in ts[2:]:
                        reduce_max(L, i + 2, t)
                    if 14 <= i + 3 < NUNIT:
                        mla_low(L, i + 3)
                    if i >= 1:
                        output_rows(L, i - 1)
                    if 14 <= i + 4 < NUNIT:
                        mla_rope(L, i + 4)

            def finish(L):
                gs = range(2) if L < DEPTH - 1 else [1]
                for g in gs:
                    for k in range(KD):
                        use = ("hT", L, g, k)
                        dve.wait_ge(hi_ready, N_HI[use])
                        nc.vector.tensor_tensor(h_t[:, 1, k, tokens(g)], bank(use)[:, 0:len(GROUPS[g]) * P],
                                                h_t[:, 0, k, tokens(g)].bitcast(F32), ALU.subtract).then_inc(free_dve, 1)
                dve.wait_ge(free_act, N_FREE_ACT["gt", L, 1, 1])
                dve.wait_ge(x_in, NX[1 + L])

                def residual(h, n, t):
                    use = ("y", L, h, t)
                    dst = xb[:, t, h * 512:(h + 1) * 512]
                    dve.wait_ge(filled, USE[use] + 1)
                    nc.vector.tensor_tensor(scr[:, n % 2, :], bank(use), ends[:, int(t >= CT), h * 512:(h + 1) * 512],
                                            ALU.mult).then_inc(free_dve, 1)
                    dve.wait_ge(free_dve, N_FREE_DVE[use])
                    chain(nc.vector.scalar_tensor_tensor(out=dst, in0=dst, scalar=ALPHA, in1=scr[:, n % 2, :],
                                                         op0=ALU.mult, op1=ALU.add))

                def scale_row(t):
                    chain(normalize(xb[:, t, :], t, ("out", L, t)))
                    nc.vector.tensor_tensor(xb[:, t, :], xb[:, t, :], ends[:, 2, :], ALU.mult).then_inc(scaled, 1)

                ts = q_tiles(L)
                for n, t in enumerate(ts):
                    residual(0, n, t)
                dve.wait_ge(ends_in, 32 * (L + 1))
                for n, t in enumerate(ts):
                    residual(1, n, t)
                    layer_stats(xb[:, t, :], t, ("out", L, t))
                    if n:
                        scale_row(ts[n - 1])
                scale_row(ts[-1])

            def lambda_dots():
                dve.wait_ge(consts_in, N_CONST)
                for L in range(DEPTH):
                    for i in range(2):
                        at = 2 * L + i
                        op = nc.vector.tensor_tensor_reduce(out=scr[:, 0, 32 * at:32 * at + 32], in0=lam_in[:, L, 2 * i, :],
                                                            in1=lam_in[:, L, 2 * i + 1, :], scale=1.0, scalar=0.0, op0=ALU.mult,
                                                            op1=ALU.add, accum_out=lam[:, L, i:i + 1])
                op.then_inc(lam_dots, 1)
                dve.wait_ge(lam_dots, 1)

            nc.vector.memset(ones_r[:].bitcast(F32), 1.0).then_inc(dve_const, 1)
            for L in range(DEPTH):
                if L == 0:
                    dve.wait_ge(x_in, NX[0])
                else:
                    dve.wait_ge(x_new, len(N_NEW) - len(q_tiles(L)))
                for t in range(TILES):
                    layer_stats(xb[:, t, :], t, ("ln", L, t))
                if L:
                    dve.wait_ge(stored, 16 * TILES)
                for t in range(TILES):
                    normalize(xb[:, t, :], t, ("ln", L, t)).then_inc(xn_ready, 1)
                use = ("adaT", L)
                dve.wait_ge(filled, USE[use] + 1)
                turned = bank(use)[:, 0:32].rearrange("p (j s) -> p j s", s=2)
                nc.vector.tensor_copy(ada_col[:, 0:8, :], turned[:, 0:8, :])
                nc.vector.tensor_scalar(ada_col[:, 8:16, :], turned[:, 8:16, :], 1.0, None, ALU.add).then_inc(free_dve, 1)
                for g in range(2):
                    for k in range(KD):
                        n = N_H[L, g, k]
                        src = area_z[:, n % 2, 0:len(GROUPS[g]) * P]
                        dve.wait_ge(free_act, N_FREE_ACT["xT", L, g, k])
                        chain(nc.vector.tensor_copy(h_t[:, 0, k, tokens(g)], src))
                        nc.vector.tensor_tensor(h_t[:, 1, k, tokens(g)], src, h_t[:, 0, k, tokens(g)].bitcast(F32),
                                                ALU.subtract).then_inc(h_ready, 1)
                if L == 0:
                    lambda_dots()
                gqa_rows(L)
                copy_blocks(L, 0)
                diff_rows(L)
                copy_blocks(L, 4)
                mla_rows(L)
                compressed_lo(L)
                attend(L)
                finish(L)


_INS = ["x", "c", "ctx", "c_ctx", "w_ada", "b_ada", "w_in", "gqa_q_g", "gqa_k_g", "diff_lq1", "diff_lk1", "diff_lq2",
        "diff_lk2", "diff_subln_g", "mla_q_g", "w_uq", "mla_kv_g", "w_ukv", "w_out", "ln_g", "ln_b"]


def rope_rows(dim):
    half = dim // 2
    freqs = (np.float32(10000.0) ** (-np.arange(0, half, 2, dtype=np.float32) / np.float32(half))).astype(np.float32)
    at = np.arange(NLAT)
    tabs = []
    for pos in (at // GRID_W, at % GRID_W):
        ang = pos.astype(np.float32)[:, None] * freqs[None, :]
        tabs.append((np.cos(ang).astype(np.float32), np.sin(ang).astype(np.float32)))
    (cr, sr), (cc, sc) = tabs
    return np.stack([np.concatenate([cr, cr, cc, cc], 1), np.concatenate([-sr, sr, -sc, sc], 1)])


def kernel(**inputs):
    import concourse.bacc as _bacc
    from concourse.bass_utils import run_bass_kernel_spmd as _run

    nc = _bacc.Bacc("TRN2", target_bir_lowering=False, num_devices=1, dynamic_dma_scratch_size=1024)
    arrays, args = {}, {}
    for name in _INS:
        arrays[f"in_{name}_dram"] = np.ascontiguousarray(inputs[name])
    arrays["rope64_dram"] = rope_rows(64)
    arrays["rope32_dram"] = rope_rows(32)
    arrays["rope_t_dram"] = np.ascontiguousarray(rope_rows(32).transpose(0, 2, 1).reshape(64, NLAT))
    for key, a in arrays.items():
        args[key] = nc.dram_tensor(key, a.shape, mybir.dt.from_np(a.dtype), kind="ExternalInput").ap()
    out = nc.dram_tensor("out_0_dram", (1, NLAT, D), F32, kind="ExternalOutput").ap()
    g = {name: args[f"in_{name}_dram"] for name in _INS}
    hybrid_layers(nc, g["x"], g["c"], g["ctx"], g["c_ctx"], g["w_ada"], g["b_ada"], g["w_in"], g["gqa_q_g"], g["gqa_k_g"],
                  [g["diff_lq1"], g["diff_lk1"], g["diff_lq2"], g["diff_lk2"]], g["diff_subln_g"], g["mla_q_g"], g["w_uq"],
                  g["mla_kv_g"], g["w_ukv"], g["w_out"], g["ln_g"], g["ln_b"],
                  args["rope64_dram"], args["rope32_dram"], args["rope_t_dram"], out)
    r = _run(nc, [arrays], core_ids=[0])
    return r.results[0]["out_0_dram"]
```
